# Optimizing a Trainium2 kernel written in Bass

```python
import jax, jax.numpy as jnp
from jax import lax
import numpy as np

D_MODEL = 2048
BATCH = 1
SEQ = 256
DEPTH = 1

POOL_WINDOWS = (2, 4, 8, 16)
POOL_GROUP = D_MODEL // 8
POOL_WIDTH = POOL_GROUP * len(POOL_WINDOWS)
ATTN_HEADS = 16
ATTN_KV_HEADS = 4
ATTN_HEAD_DIM = 64
ATTN_WINDOW = 128
ATTN_BLOCK = 128
Q_WIDTH = ATTN_HEADS * ATTN_HEAD_DIM
KV_WIDTH = ATTN_KV_HEADS * ATTN_HEAD_DIM
RET_HEADS = 4
RET_KEY_DIM = 256
RET_VALUE_DIM = 512
RET_CHUNK = 128
RQK_WIDTH = RET_HEADS * RET_KEY_DIM
RV_WIDTH = RET_HEADS * RET_VALUE_DIM
FFN_HIDDEN = 5632
RMS_EPS = 1e-6
N_BRANCHES = 3

IN_SPLITS = (POOL_WIDTH, Q_WIDTH, KV_WIDTH, KV_WIDTH, RQK_WIDTH, RQK_WIDTH, RV_WIDTH, RV_WIDTH)
IN_WIDTH = int(sum(IN_SPLITS))
IN_OFFSETS = tuple(int(o) for o in np.cumsum(IN_SPLITS)[:-1])

kernel_name = "hybrid_gated_pool_swa_retention_macaron"

def rms_norm(x, g):
    xf = x.astype(jnp.float32)
    y = xf * lax.rsqrt(jnp.mean(xf * xf, axis=-1, keepdims=True) + RMS_EPS)
    return (y * g.astype(jnp.float32)).astype(x.dtype)

def swiglu(x, w_up, w_down):
    g, u = jnp.split(x @ w_up, 2, axis=-1)
    return (jax.nn.silu(g) * u) @ w_down

def pool_mixer(xp, w_group, scale):
    B, S, _ = xp.shape
    xf = xp.astype(jnp.float32)
    cs = jnp.concatenate([jnp.zeros((B, 1, POOL_WIDTH), jnp.float32), jnp.cumsum(xf, axis=1)], axis=1)
    t = jnp.arange(S)
    groups = []
    for gi, w in enumerate(POOL_WINDOWS):
        sl = slice(gi * POOL_GROUP, (gi + 1) * POOL_GROUP)
        start = jnp.maximum(t + 1 - w, 0)
        window_sum = cs[:, 1:, sl] - cs[:, start, sl]
        count = (t + 1 - start).astype(jnp.float32)[None, :, None]
        groups.append(window_sum / count - xf[:, :, sl])
    pooled = jnp.stack(groups, axis=2).astype(xp.dtype)
    mixed = jnp.einsum('bsgc,gcd->bsgd', pooled, w_group)
    return mixed.reshape(B, S, POOL_WIDTH) * scale

def sliding_window_attention(q, k, v, sinks):
    B, S, _ = q.shape
    NB = S // ATTN_BLOCK
    G = ATTN_HEADS // ATTN_KV_HEADS
    qb = q.reshape(B, NB, ATTN_BLOCK, ATTN_KV_HEADS, G, ATTN_HEAD_DIM)
    kb = k.reshape(B, NB, ATTN_BLOCK, ATTN_KV_HEADS, ATTN_HEAD_DIM)
    vb = v.reshape(B, NB, ATTN_BLOCK, ATTN_KV_HEADS, ATTN_HEAD_DIM)

    def with_prev(xb):
        prev = jnp.concatenate([jnp.zeros_like(xb[:, :1]), xb[:, :-1]], axis=1)
        return jnp.concatenate([prev, xb], axis=2)

    kk, vv = with_prev(kb), with_prev(vb)
    scores = jnp.einsum('bnqhgd,bnkhd->bhgnqk', qb, kk).astype(jnp.float32) * (ATTN_HEAD_DIM ** -0.5)
    qi = jnp.arange(ATTN_BLOCK)[:, None]
    ki = jnp.arange(2 * ATTN_BLOCK)[None, :]
    dist = qi + ATTN_BLOCK - ki
    key_pos = jnp.arange(NB)[:, None, None] * ATTN_BLOCK - ATTN_BLOCK + ki[None]
    valid = (dist >= 0) & (dist < ATTN_WINDOW) & (key_pos >= 0)
    slopes = jnp.exp2(-8.0 * jnp.arange(1, ATTN_HEADS + 1, dtype=jnp.float32) / ATTN_HEADS)
    alibi = -slopes.reshape(ATTN_KV_HEADS, G)[:, :, None, None, None] * dist.astype(jnp.float32)
    scores = jnp.where(valid, scores + alibi, -jnp.inf)
    sink = sinks.astype(jnp.float32).reshape(ATTN_KV_HEADS, G)[:, :, None, None, None]
    m = jnp.maximum(jnp.max(scores, axis=-1, keepdims=True), sink)
    p = jnp.exp(scores - m)
    p = p / (jnp.sum(p, axis=-1, keepdims=True) + jnp.exp(sink - m))
    out = jnp.einsum('bhgnqk,bnkhd->bnqhgd', p.astype(v.dtype), vv)
    return out.reshape(B, S, Q_WIDTH)

def retention(q, k, v):
    B, S = q.shape[0], q.shape[1]
    NC = S // RET_CHUNK
    log_g = jnp.log(1.0 - jnp.exp2(-5.0 - jnp.arange(RET_HEADS, dtype=jnp.float32)))
    k = k * (RET_KEY_DIM ** -0.5)

    def chunks(a):
        return a.reshape(B, NC, RET_CHUNK, RET_HEADS, a.shape[-1]).transpose(1, 0, 3, 2, 4)

    qc, kc, vc = chunks(q), chunks(k), chunks(v)
    pos = jnp.arange(RET_CHUNK, dtype=jnp.float32)
    diff = pos[:, None] - pos[None, :]
    intra = jnp.where(diff >= 0, jnp.exp(log_g[:, None, None] * jnp.maximum(diff, 0.0)), 0.0)
    q_decay = jnp.exp(log_g[:, None] * (pos + 1.0))[..., None]
    k_decay = jnp.exp(log_g[:, None] * (RET_CHUNK - 1.0 - pos))[..., None]
    chunk_decay = jnp.exp(log_g * RET_CHUNK)[:, None, None]

    def step(state, xs):
        qi, ki, vi = xs
        inner = jnp.einsum('bhid,bhjd->bhij', qi, ki) * intra
        o = jnp.einsum('bhij,bhjv->bhiv', inner, vi) + jnp.einsum('bhid,bhdv->bhiv', qi * q_decay, state)
        state = state * chunk_decay + jnp.einsum('bhjd,bhjv->bhdv', ki * k_decay, vi)
        return state, o

    state0 = jnp.zeros((B, RET_HEADS, RET_KEY_DIM, RET_VALUE_DIM), jnp.float32)
    _, o = lax.scan(step, state0, (qc, kc, vc))
    return o.transpose(1, 0, 3, 2, 4).reshape(B, S, RET_HEADS, RET_VALUE_DIM)

def hybrid_mixer(u, w_in, pool_w, pool_scale, attn_sinks, ret_norm,
                 w_pool_out, w_attn_out, w_ret_out, w_gate, w_out):
    B, S, _ = u.shape
    xp, q, k, v, rq, rk, rv, rg = jnp.split(u @ w_in, IN_OFFSETS, axis=-1)
    pool_out = pool_mixer(xp, pool_w, pool_scale) @ w_pool_out
    attn_out = sliding_window_attention(q, k, v, attn_sinks) @ w_attn_out
    f32 = jnp.float32
    o = retention(rq.reshape(B, S, RET_HEADS, RET_KEY_DIM).astype(f32),
                  rk.reshape(B, S, RET_HEADS, RET_KEY_DIM).astype(f32),
                  rv.reshape(B, S, RET_HEADS, RET_VALUE_DIM).astype(f32))
    o = o * lax.rsqrt(jnp.mean(o * o, axis=-1, keepdims=True) + RMS_EPS)
    o = o.reshape(B, S, RV_WIDTH) * ret_norm.astype(f32)
    ret_out = (jax.nn.silu(rg.astype(f32)) * o).astype(u.dtype) @ w_ret_out
    g_pool, g_attn, g_ret = jnp.split(jax.nn.sigmoid((u @ w_gate).astype(f32)).astype(u.dtype), N_BRANCHES, axis=-1)
    merged = g_pool * pool_out + g_attn * attn_out + g_ret * ret_out
    return merged @ w_out

def setup_inputs(seed: int = 0) -> dict:
    key = jax.random.key(seed)
    ks = jax.random.split(key, 32)
    f32 = jnp.float32

    def dense(k, shape, fan_in):
        return jax.random.normal(k, shape, f32) * (fan_in ** -0.5)

    def gain(k, shape):
        return 1.0 + 0.05 * jax.random.normal(k, shape, f32)

    L, D, F = DEPTH, D_MODEL, FFN_HIDDEN
    return {
        "x": jax.random.normal(ks[0], (BATCH, SEQ, D), f32),
        "ffn1_pre": gain(ks[1], (L, D)),
        "ffn1_up": dense(ks[2], (L, D, 2 * F), D),
        "ffn1_down": dense(ks[3], (L, F, D), F),
        "ffn1_post": gain(ks[4], (L, D)),
        "mix_pre": gain(ks[5], (L, D)),
        "w_in": dense(ks[6], (L, D, IN_WIDTH), D),
        "pool_w": dense(ks[7], (L, len(POOL_WINDOWS), POOL_GROUP, POOL_GROUP), POOL_GROUP),
        "pool_scale": gain(ks[8], (L, POOL_WIDTH)),
        "attn_sinks": jax.random.normal(ks[9], (L, ATTN_HEADS), f32),
        "ret_norm": gain(ks[10], (L, RV_WIDTH)),
        "w_pool_out": dense(ks[11], (L, POOL_WIDTH, D), POOL_WIDTH),
        "w_attn_out": dense(ks[12], (L, Q_WIDTH, D), Q_WIDTH),
        "w_ret_out": dense(ks[13], (L, RV_WIDTH, D), RV_WIDTH),
        "w_gate": dense(ks[14], (L, D, N_BRANCHES * D), D),
        "w_out": dense(ks[15], (L, D, D), D),
        "mix_post": gain(ks[16], (L, D)),
        "ffn2_pre": gain(ks[17], (L, D)),
        "ffn2_up": dense(ks[18], (L, D, 2 * F), D),
        "ffn2_down": dense(ks[19], (L, F, D), F),
        "ffn2_post": gain(ks[20], (L, D)),
    }

def reference(x, ffn1_pre, ffn1_up, ffn1_down, ffn1_post, mix_pre, w_in, pool_w, pool_scale,
              attn_sinks, ret_norm, w_pool_out, w_attn_out, w_ret_out, w_gate, w_out, mix_post,
              ffn2_pre, ffn2_up, ffn2_down, ffn2_post):
    h = x
    for l in range(DEPTH):
        h = h + 0.5 * rms_norm(swiglu(rms_norm(h, ffn1_pre[l]), ffn1_up[l], ffn1_down[l]), ffn1_post[l])
        mix = hybrid_mixer(rms_norm(h, mix_pre[l]), w_in[l], pool_w[l], pool_scale[l], attn_sinks[l],
                           ret_norm[l], w_pool_out[l], w_attn_out[l], w_ret_out[l], w_gate[l], w_out[l])
        h = h + rms_norm(mix, mix_post[l])
        h = h + 0.5 * rms_norm(swiglu(rms_norm(h, ffn2_pre[l]), ffn2_up[l], ffn2_down[l]), ffn2_post[l])
    return h


_drawn_inputs = setup_inputs


def setup_inputs(seed=0):
    import zlib

    import numpy as np

    out = dict(_drawn_inputs(seed))
    spreads = {}
    factors = {'ret_norm': 3.008, 'ffn2_post': 3.634, 'pool_scale': 3.216, 'attn_sinks': 2.86}
    for name, (base, spread) in spreads.items():
        noise = np.random.default_rng([zlib.crc32(name.encode()), seed]).standard_normal(out[name].shape)
        drawn = base * np.exp(spread * noise) if base else spread * noise
        out[name] = __import__('jax').numpy.asarray(drawn.astype(out[name].dtype))
    for name, factor in factors.items():
        out[name] = (out[name] * factor).astype(out[name].dtype)
    return out
```

```python
import concourse.bass as bass
from concourse import mybir
from contextlib import ExitStack

P = 128
D = 2048
SEQ = 256
MT = SEQ // P
FFN = 5632
STRIP = 512
CH = D // STRIP
SLOTS = 4
KG = 2
EPS = 1e-6

POOL_WINDOWS = (2, 4, 8, 16)
PG = 256
HEADS = 16
KVH = 4
QPK = HEADS // KVH
DH = 64
RKD = 256
RVD = 512
OFF_XP, OFF_K, OFF_RQ, OFF_RV, OFF_RG = 0, 2048, 2560, 4608, 6656

KD, KF = D // P, FFN // P
GD = KD // KG
GF = KF // KG
GH = GD // 2
NUP = FFN // STRIP

SECTIONS = [("up0", NUP, 2 * GD, 2), ("down0", CH // 2, 2 * GF, 2),
            ("kv", 1, GD, 1), ("heads", KVH, 4 * GD, 4), ("merge", CH, 4 * GD + 2 * GH, 6), ("out", CH // 2, 2 * GD, 2),
            ("up1", NUP, 2 * GD, 2), ("down1", CH // 2, 2 * GF, 2)]


def section_starts():
    groups, strips, g, s = {}, {}, 0, 0
    for name, iters, ng, ns in SECTIONS:
        groups[name], strips[name] = (g, ng), (s, ns)
        g, s = g + iters * ng, s + iters * ns
    return groups, strips


SPLIT_PIECES = ("x0", "x1", "x2", "merged", "hidden0", "hidden1", "ret", "pool", "pv1", "pv0")


def bank_uses():
    uses, count = {}, [0, 0, 0, 0]
    splits, count_split = {}, [0, 0, 0, 0]

    def use(piece, *banks):
        for b in banks:
            uses.setdefault((piece, b), []).append(count[b])
            count[b] += 1
            if piece in SPLIT_PIECES:
                splits.setdefault((piece, b), []).append(count_split[b])
                count_split[b] += 1

    def transposed(name):
        for c in range(CH):
            use(name, *((0, 1) if c % 2 == 0 else (2, 3)))

    def up_down(f):
        for _ in range(NUP):
            use(f"hidden{f}", 0, 1)

    transposed("x0")
    up_down(0)
    transposed("x1")
    use("k", 0, 1, 2, 3)
    for g in range(KVH):
        if g:
            use("ret", 0, 1)
        use("q", 0), use("window", 2)
        use("score1", 2, 3), use("pool", 1)
        use("probT1", 2, 3)
        use("pv1", 1), use("score0", 2)
        use("rk", 3), use("rq", 0)
        use("inner", 0)
        use("probT0", 2)
        use("pv0", 1)
        use("o", 2, 3)
    use("ret", 0, 1)
    transposed("merged")
    transposed("x2")
    up_down(1)
    return uses, splits


def hybrid_trunk(nc, t, out):
    f32, f32r = mybir.dt.float32, mybir.dt.float32r
    ALU, ACT, AX = mybir.AluOpType, mybir.ActivationFunctionType, mybir.AxisListType
    ds = bass.ds
    G0, S0 = section_starts()
    USES, SPLITS = bank_uses()

    def grouped(w):
        return w.rearrange("(g kk p) n -> g p kk n", kk=KG, p=P)

    up = [grouped(t["ffn1_up"][0]), grouped(t["ffn2_up"][0])]
    down = [grouped(t["ffn1_down"][0]), grouped(t["ffn2_down"][0])]
    w_in = grouped(t["w_in"][0])
    w_gate, w_out = grouped(t["w_gate"][0]), grouped(t["w_out"][0])
    w_branch = [grouped(t[n][0]) for n in ("w_pool_out", "w_attn_out", "w_ret_out")]

    ctx = ExitStack()
    with ctx:
        place = {"at": 16512}

        def sb(name, shape, dt, at=None):
            size = 4
            for n in shape[1:]:
                size *= n
            if at is None:
                at = place["at"]
                place["at"] += -(-size // 32) * 32
            return nc.alloc_sbuf_tensor_at(name, shape, dt, offset=at)

        h = sb("h", [P, MT, D], f32)
        x_at = place["at"]
        xT_hi = sb("xT_hi", [P, KD, SEQ], f32r)
        xT_lo = sb("xT_lo", [P, KD, SEQ], f32r)
        w_raw = sb("w_raw", [P, SLOTS, KG * STRIP], f32)
        w_hi = sb("w_hi", [P, SLOTS, KG * STRIP], f32r)
        w_lo = sb("w_lo", [P, SLOTS, KG * STRIP], f32r)
        tmp_at = place["at"]
        gate_sb = sb("gate_sb", [P, MT, STRIP], f32)
        hid_sb = sb("hid_sb", [P, MT, STRIP], f32)
        junk = sb("junk", [P, D], f32, at=tmp_at)
        ident = sb("ident", [P, P], f32)
        dist = sb("dist", [P, 2 * P], f32)
        pre_gain = sb("pre_gain", [P, 3, KD], f32)
        ret_gain = sb("ret_gain", [P, KD], f32)
        pool_gain = sb("pool_gain", [P, KD // 2], f32)
        neg_slope = sb("neg_slope", [P, HEADS], f32)
        sink = sb("sink", [P, HEADS], f32)
        neg_sink = sb("neg_sink", [P, HEADS], f32)
        sq_pre = sb("sq_pre", [P, MT], f32)
        sq_strip = sb("sq_strip", [P, 2, MT], f32)
        sq_post = sb("sq_post", [P, 3, MT], f32)
        sq_o = sb("sq_o", [P, MT], f32)
        mean_sq = sb("mean_sq", [P, 7, MT], f32)
        rs_pre = sb("rs_pre", [P, 3, MT], f32)
        rs_post = sb("rs_post", [P, 3, MT], f32)
        rs_o = sb("rs_o", [P, MT], f32)
        minus_half = sb("minus_half", [P, MT], f32)
        neg_max = sb("neg_max", [P, QPK], f32)
        sink_arg = sb("sink_arg", [P, QPK], f32)
        sink_exp = sb("sink_exp", [P, QPK], f32)
        den = sb("den", [P, QPK], f32)
        rden = sb("rden", [P, QPK], f32)
        r = place["at"]
        act_hi = sb("act_hi", [P, KF, SEQ], f32r, at=r)
        act_lo = sb("act_lo", [P, KF, SEQ], f32r, at=r + 4 * KF * SEQ)
        post_gain = sb("post_gain", [P, D], f32, at=r + 8 * KF * SEQ)
        assert r + 8 * KF * SEQ + 4 * D <= nc.sbuf_usable_end
        y_ffn = sb("y_ffn", [P, CH, MT, STRIP], f32, at=x_at)
        place["at"] = r
        retT_hi = sb("retT_hi", [P, KD, SEQ], f32r)
        retT_lo = sb("retT_lo", [P, KD, SEQ], f32r)
        attT_hi = sb("attT_hi", [P, KD // 2, SEQ], f32r)
        attT_lo = sb("attT_lo", [P, KD // 2, SEQ], f32r)
        poolT_hi = sb("poolT_hi", [P, KD // 2, SEQ], f32r)
        poolT_lo = sb("poolT_lo", [P, KD // 2, SEQ], f32r)
        m_at = place["at"]
        kT = sb("kT", [P, 2, KVH, SEQ], f32)
        v_sb = sb("v_sb", [P, MT, KVH * DH], f32)
        v_now = sb("v_now", [P, MT, 3 * DH], f32)
        s_at = place["at"]
        s_sb = sb("s_sb", [P, QPK, 2 * P], f32)
        pT = sb("pT", [P, QPK, 2 * P], f32)
        k_pad = sb("k_pad", [P, MT, KVH, 3 * DH], f32, at=s_at)
        o_junk = sb("o_junk", [P, STRIP], f32, at=s_at)
        qT = sb("qT", [P, 2, SEQ], f32)
        winT = sb("winT", [P, 2, SEQ], f32)
        rqT = sb("rqT", [P, 2, SEQ], f32)
        rkT = sb("rkT", [P, 2, SEQ], f32)
        innerT = sb("innerT", [P, 3 * P], f32)
        decay = sb("decay", [P, 2 * P], f32)
        band = sb("band", [P, 3 * P], f32)
        pool_w = sb("pool_w", [P, 2, PG], f32)
        assert place["at"] <= nc.sbuf_usable_end
        merged = sb("merged", [P, CH, MT, STRIP], f32, at=m_at)
        y_mix = sb("y_mix", [P, CH, MT, STRIP], f32, at=m_at)
        assert m_at + 4 * CH * MT * STRIP <= r + 8 * KF * SEQ
        ys = [y_ffn, y_mix, y_ffn]

        acc = [[ctx.enter_context(nc.psum_tensor(f"acc{q}{m}", [P, STRIP], f32)) for m in range(MT)] for q in range(2)]
        bank = [ctx.enter_context(nc.psum_tensor(f"bank{b}", [P, STRIP], f32)) for b in range(4)]

        def sem(name):
            return ctx.enter_context(nc.semaphore(name))

        w_landed = [sem(f"w_landed{s}") for s in range(SLOTS)]
        block1_landed = [sem(f"block1_landed{s}") for s in range(SLOTS)]
        w_rounded = sem("w_rounded")
        w_split = sem("w_split")
        w_used = sem("w_used")
        acc_read = [sem(f"acc_read{q}") for q in range(2)]
        filled = [sem(f"bank_filled{b}") for b in range(4)]
        read = [sem(f"bank_read{b}") for b in range(4)]
        rounded = [sem(f"bank_rounded{b}") for b in range(4)]
        x_landed = sem("x_landed")
        consts_landed = sem("consts_landed")
        gain_landed = sem("gain_landed")
        tables_landed = sem("tables_landed")
        out_landed = sem("out_landed")
        setup_done = sem("setup_done")
        pads_zeroed = sem("pads_zeroed")
        silu_done = sem("silu_done")
        h_ready = sem("h_ready")
        squares = sem("squares")
        sq_added = sem("sq_added")
        mean_ready = sem("mean_ready")
        rs_ready = sem("rs_ready")
        max_ready = sem("max_ready")
        exp_done = sem("exp_done")
        prob_ready = sem("prob_ready")
        o_squares = sem("o_squares")
        ret_ready = sem("ret_ready")
        dve_step = sem("dve_step")

        def group(sec, i, n):
            return G0[sec][0] + i * G0[sec][1] + n

        def group_landed(sec, i, n):
            assert G0[sec][0] % SLOTS == 0 and G0[sec][1] % SLOTS == 0
            return 16 * (G0[sec][0] // SLOTS + i * (G0[sec][1] // SLOTS) + n // SLOTS + 1)

        def two_blocks(n):
            return n < 2 * GD

        def block_landed(g, n):
            return 16 * (g * (2 * GD // SLOTS) + n // SLOTS + 1)

        def before(i, iters):
            return nc.s_assert_within(i - 1, 0, iters - 2, skip_runtime_bounds_check_because="it stands inside If(i > 0)")

        def pair_of(sec, k):
            return (S0[sec][0] + k) % 2

        def strip_in_pair(sec, i, k):
            return (S0[sec][0] + k) // 2 + i * (S0[sec][1] // 2)

        def use(piece, b, n=0, of=USES):
            u = of[piece, b]
            step = u[1] - u[0] if len(u) > 1 else 0
            assert all(u[j] == u[0] + j * step for j in range(len(u)))
            return u[0] + n * step

        def wait_strip(eng, sec, i, n):
            eng.wait_ge(w_used, group(sec, i, n) + 1 + SLOTS)

        def wait_strip_read(eng, sec, i, k):
            eng.wait_ge(acc_read[pair_of(sec, k)], strip_in_pair(sec, i, k) + 2)

        def wait_filled(eng, piece, b, n=0):
            eng.wait_ge(filled[b], use(piece, b, n) + 1)

        def wait_read(eng, piece, b, n=0):
            eng.wait_ge(read[b], use(piece, b, n) + 2)

        def wait_rounded(eng, piece, b, n=0):
            eng.wait_ge(rounded[b], use(piece, b, n, SPLITS) + 1)

        def chunk_bank(k):
            return k % 4, k // 4

        MEAN = {"pre0": 0, "post0": 1, "pre1": 2, "o": 3, "post1": 3 + KVH, "pre2": 4 + KVH, "post2": 5 + KVH}
        MEAN_ROW = {"pre0": 0, "post0": 1, "pre1": 2, "o": 3, "post1": 4, "pre2": 5, "post2": 6}
        SQUARES, at = {}, 0
        for name, sets in (("pre0", 1), ("down0", CH), ("pre1", 1), ("out", CH), ("pre2", 1), ("down1", CH)):
            SQUARES[name], at = at, at + sets * MT
        NCONST = 9
        block = ctx.enter_context(nc.Block())

        @block.sync
        def _(sp):
            def load(sec, i, n, src):
                s = n % SLOTS
                sp.wait_ge(w_split, group(sec, i, n) + 1)
                sp.dma_start(slot(s), src).then_inc(w_landed[s], 16)

            def slot(s):
                return w_raw[:, s, :].rearrange("p (kk n) -> p kk n", kk=KG)

            def load_two_blocks(sec, i, n, src0, src1):
                s, half = n % SLOTS, STRIP // 2
                sp.wait_ge(w_split, group(sec, i, n) + 1)
                sp.dma_start(slot(s)[:, :, 0:half], src0).then_inc(w_landed[s], 16)
                sp.dma_start(slot(s)[:, :, half:], src1).then_inc(block1_landed[s], 16)

            def up_loads(f):
                with sp.Fori(0, NUP) as i:
                    for n in range(2 * GD):
                        col = i * STRIP + (n // GD) * FFN
                        load(f"up{f}", i, n, up[f][n % GD][:, :, ds(col, STRIP)])

            def down_loads(f):
                with sp.Fori(0, CH // 2) as i:
                    for n in range(2 * GF):
                        load(f"down{f}", i, n, down[f][n % GF][:, :, ds((2 * i + n // GF) * STRIP, STRIP)])

            sp.dma_start(h[:, :, :], t["x"][0].rearrange("(m p) n -> p m n", p=P)).then_inc(x_landed, 16)
            up_loads(0)
            down_loads(0)
            for n in range(GD):
                load("kv", 0, n, w_in[n][:, :, OFF_K:OFF_K + STRIP])
            with sp.Fori(0, KVH) as g:
                for n in range(4 * GD):
                    strip, k = n // GD, n % GD
                    if strip < 2:
                        off = OFF_XP if strip == 0 else OFF_RQ
                        load_two_blocks("heads", g, n, w_in[k][:, :, ds(g * PG + off, PG)],
                                        w_in[k][:, :, ds(g * PG + (off + KVH * PG), PG)])
                    else:
                        off = OFF_RV if strip == 2 else OFF_RG
                        load("heads", g, n, w_in[k][:, :, ds(g * RVD + off, STRIP)])
            with sp.Fori(0, CH) as c:
                n = 0
                for br in range(3):
                    for k in range(GD):
                        load("merge", c, n, w_gate[k][:, :, ds(c * STRIP + br * D, STRIP)])
                        n += 1
                    for k in range(GD if br == 2 else GH):
                        load("merge", c, n, w_branch[br][k][:, :, ds(c * STRIP, STRIP)])
                        n += 1
            with sp.Fori(0, CH // 2) as i:
                for n in range(2 * GD):
                    load("out", i, n, w_out[n % GD][:, :, ds((2 * i + n // GD) * STRIP, STRIP)])
            up_loads(1)
            down_loads(1)
            for c in range(CH):
                sp.wait_ge(h_ready, MT * (CH * 2 + c + 1))
                sp.dma_start(out[0].rearrange("(m p) n -> p m n", p=P)[:, :, c * STRIP:(c + 1) * STRIP],
                             h[:, :, c * STRIP:(c + 1) * STRIP]).then_inc(out_landed, 16)
            sp.wait_ge(out_landed, 16 * CH)

        @block.gpsimd
        def _(pool):
            def per_k_tile(v):
                return v.rearrange("(k p) -> p k", p=P)

            def on_all(v, n):
                return v.rearrange("(a n) -> a n", a=1).broadcast_to([P, n])

            ctx.enter_context(nc.allow_non_contiguous_dma(reason="a few KB of gains, one element for each partition"))
            pool.dma_start(ident[:, :], t["c_ident"]).then_inc(consts_landed, 16)
            for f, name in enumerate(("ffn1_pre", "mix_pre", "ffn2_pre")):
                pool.dma_start(pre_gain[:, f, :], per_k_tile(t[name][0])).then_inc(consts_landed, 16)
            pool.dma_start(ret_gain[:, :], per_k_tile(t["ret_norm"][0])).then_inc(consts_landed, 16)
            pool.dma_start(pool_gain[:, :], per_k_tile(t["pool_scale"][0])).then_inc(consts_landed, 16)
            pool.dma_start(dist[:, :], t["c_dist"]).then_inc(consts_landed, 16)
            pool.dma_start(neg_slope[:, :], t["c_neg_slope"]).then_inc(consts_landed, 16)
            pool.dma_start(sink[:, :], on_all(t["attn_sinks"][0], HEADS)).then_inc(consts_landed, 16)
            pool.memset(minus_half[:, :], -0.5).then_inc(setup_done, 1)
            pool.dma_start(post_gain[:, :], on_all(t["ffn1_post"][0], D)).then_inc(gain_landed, 16)
            pool.wait_ge(setup_done, 1)

            def rsqrt(what, dst, g=0):
                pool.wait_ge(mean_ready, MEAN[what] + g + 1)
                pool.tensor_tensor(dst, mean_sq[:, MEAN_ROW[what], :], minus_half[:, :], ALU.pow).then_inc(rs_ready, 1)

            rsqrt("pre0", rs_pre[:, 0, :])
            rsqrt("post0", rs_post[:, 0, :])

            wait_strip(pool, "down0", CH // 2 - 1, 2 * GF - 1)
            pool.memset(k_pad[:, :, :, :], 0.0).then_inc(pads_zeroed, 1)
            pool.memset(v_now[:, :, :], 0.0).then_inc(pads_zeroed, 1)

            def tables(g):
                pool.dma_start(decay[:, :], t["c_decay"][g]).then_inc(tables_landed, 16)
                pool.dma_start(band[:, :], t["c_band"][g]).then_inc(tables_landed, 16)
                pool.dma_start(pool_w[:, :, :], t["pool_w"][0][g].rearrange("(k p) n -> p k n", p=P)).then_inc(tables_landed, 16)

            tables(0)
            rsqrt("pre1", rs_pre[:, 1, :])
            for g in range(KVH):
                rsqrt("o", rs_o[:, :], g)
                if g + 1 < KVH:
                    tables(g + 1)
            wait_filled(pool, "o", 3, KVH - 1)
            wait_read(pool, "inner", 0, KVH - 1)
            pool.dma_start(post_gain[:, :], on_all(t["mix_post"][0], D)).then_inc(gain_landed, 16)
            rsqrt("post1", rs_post[:, 1, :])
            pool.dma_start(post_gain[:, :], on_all(t["ffn2_post"][0], D)).then_inc(gain_landed, 16)
            rsqrt("pre2", rs_pre[:, 2, :])
            rsqrt("post2", rs_post[:, 2, :])

        @block.tensor
        def _(pe):
            def products(sec, i, n, hi, lo, kt, k, first, last):
                s = n % SLOTS
                pair = acc[pair_of(sec, k)]
                if first:
                    pe.wait_ge(acc_read[pair_of(sec, k)], strip_in_pair(sec, i, k) + 1)
                pe.wait_ge(w_split, group(sec, i, n) + 1 + SLOTS)
                for kk in range(KG):
                    for m in range(MT):
                        xh = hi[:, kt + kk, m * P:(m + 1) * P]
                        xl = lo[:, kt + kk, m * P:(m + 1) * P]
                        wh = w_hi[:, s, kk * STRIP:(kk + 1) * STRIP]
                        wl = w_lo[:, s, kk * STRIP:(kk + 1) * STRIP]
                        pe.matmul(pair[m][:, :], xh, wh, start=(first and kk == 0), stop=False)
                        pe.matmul(pair[m][:, :], xh, wl, start=False, stop=False)
                        mm = pe.matmul(pair[m][:, :], xl, wh, start=False, stop=(last and kk == KG - 1))
                mm.then_inc(w_used, 1)

            def claim(piece, b, n=0):
                pe.wait_ge(read[b], use(piece, b, n) + 1)

            def transpose(dst, src):
                return pe.transpose(dst, src, ident[:, :])

            def transpose_chunks(name, src, ready):
                for k in range(GD):
                    b, n = chunk_bank(k)
                    if k % 2 == 0:
                        ready(k // 2)
                    claim(name, b, n)
                    for kk in range(2):
                        for m in range(MT):
                            last = transpose(bank[b][:, kk * SEQ + m * P:kk * SEQ + (m + 1) * P],
                                             src(k // 2, m, 2 * (k % 2) + kk))
                    last.then_inc(filled[b], 1)

            def wait_xT(name, k):
                b, n = chunk_bank(k)
                wait_read(pe, name, b, n)

            def hidden_transposes(f, p):
                sec = f"up{f}"
                wait_strip_read(pe, sec, p, 1)
                for m in range(MT):
                    claim(f"hidden{f}", m, p)
                    for k in range(4):
                        last = transpose(bank[m][:, k * P:(k + 1) * P], hid_sb[:, m, k * P:(k + 1) * P])
                    last.then_inc(filled[m], 1)

            def swiglu(f):
                with pe.Fori(0, NUP) as i:
                    for n in range(2 * GD):
                        k = n % GD
                        if n < GD:
                            wait_xT(f"x{2 * f}", k)
                        products(f"up{f}", i, n, xT_hi, xT_lo, KG * k, n // GD, k == 0, k == GD - 1)
                        if n == 1:
                            with pe.If(i > 0):
                                hidden_transposes(f, before(i, NUP))
                with pe.Fori(0, CH // 2) as i:
                    for n in range(2 * GF):
                        k = n % GF
                        if k == GF - 2:
                            for m in range(MT):
                                wait_read(pe, f"hidden{f}", m, NUP - 1)
                        products(f"down{f}", i, n, act_hi, act_lo, KG * k, n // GF, k == 0, k == GF - 1)
                        if n == 1:
                            with pe.If(i < 1):
                                hidden_transposes(f, NUP - 1)

            def h_chunk(c, m, k):
                return h[:, m, c * STRIP + k * P:c * STRIP + (k + 1) * P]

            pe.sem_inc(w_used, SLOTS)
            for b in range(4):
                pe.sem_inc(read[b], 1)
            for q in range(2):
                pe.sem_inc(acc_read[q], 1)
            pe.wait_ge(consts_landed, 16 * NCONST)
            pe.wait_ge(x_landed, 16)
            transpose_chunks("x0", h_chunk, lambda c: None)
            swiglu(0)

            transpose_chunks("x1", h_chunk, lambda c: pe.wait_ge(h_ready, MT * (c + 1)))
            for k in range(GD):
                wait_xT("x1", k)
                products("kv", 0, k, xT_hi, xT_lo, KG * k, 0, k == 0, k == GD - 1)
            wait_strip_read(pe, "kv", 0, 0)
            for b in range(4):
                m, odd = b % 2, b // 2
                claim("k", b)
                for g in range(KVH):
                    src = k_pad[:, m, g, 0:2 * DH] if odd else k_pad[:, m, g, DH:3 * DH]
                    last = transpose(bank[b][:, g * P:(g + 1) * P], src)
                last.then_inc(filled[b], 1)

            def ret_transposes(g):
                pe.wait_ge(ret_ready, g + 1)
                for half in range(2):
                    claim("ret", half, g)
                    for kk in range(2):
                        for m in range(MT):
                            k = 2 * half + kk
                            last = transpose(bank[half][:, kk * SEQ + m * P:kk * SEQ + (m + 1) * P],
                                             gate_sb[:, m, k * P:(k + 1) * P])
                    last.then_inc(filled[half], 1)

            def strip_transposes(piece, b, g, col):
                claim(piece, b, g)
                for kk in range(2):
                    for m in range(MT):
                        last = transpose(bank[b][:, kk * SEQ + m * P:kk * SEQ + (m + 1) * P],
                                         gate_sb[:, m, col + kk * P:col + (kk + 1) * P])
                last.then_inc(filled[b], 1)

            kT_of = kT[:, :, :, :]

            def scores(g, m):
                piece, w = f"score{m}", P * (m + 1)
                per_bank = STRIP // w
                for hd in range(QPK):
                    b, col = 2 + hd // per_bank, (hd % per_bank) * w
                    if hd % per_bank == 0:
                        claim(piece, b, g)
                    last = pe.matmul(bank[b][:, col:col + w], qT[:, hd // 2, m * P:(m + 1) * P],
                                     kT_of[:, hd % 2, ds(g, 1), 0:w].rearrange("p a n -> p (a n)"), start=True, stop=True)
                    if (hd + 1) % per_bank == 0:
                        last.then_inc(filled[b], 1)

            def prob_transposes(g, m):
                piece, blocks = f"probT{m}", m + 1
                per_bank = 4 // blocks
                pe.wait_ge(prob_ready, 2 * g + (1 if m == 1 else 2))
                for hd in range(QPK):
                    b = 2 + hd // per_bank
                    if hd % per_bank == 0:
                        claim(piece, b, g)
                    for j in range(blocks):
                        col = ((hd % per_bank) * blocks + j) * P
                        last = transpose(bank[b][:, col:col + P], s_sb[:, hd, j * P:(j + 1) * P])
                    if (hd + 1) % per_bank == 0:
                        last.then_inc(filled[b], 1)

            def prob_values(g, m):
                piece = f"pv{m}"
                claim(piece, 1, g)
                for pair in range(2):
                    n = 0
                    for odd in range(2):
                        for j in range(m + 1):
                            lhsT = v_now[:, j, 0:2 * DH] if odd else v_now[:, j, DH:3 * DH]
                            last = pe.matmul(bank[1][:, pair * P:(pair + 1) * P], lhsT,
                                             pT[:, 2 * pair + odd, j * P:(j + 1) * P],
                                             start=(n == 0), stop=(n == 2 * m + 1))
                            n += 1
                last.then_inc(filled[1], 1)

            with pe.Fori(0, KVH) as g:
                for n in range(4 * GD):
                    k = n % GD
                    products("heads", g, n, xT_hi, xT_lo, KG * k, n // GD, k == 0, k == GD - 1)
                    if n == 3:
                        with pe.If(g > 0):
                            ret_transposes(before(g, KVH))
                    if n == 8:
                        wait_strip_read(pe, "heads", g, 0)
                        strip_transposes("q", 0, g, PG)
                        claim("window", 2, g)
                        pe.wait_ge(tables_landed, 48 * (g + 1))
                        for ct in range(2):
                            col = ct * SEQ
                            pe.matmul(bank[2][:, col:col + SEQ], gate_sb[:, 0, ct * P:(ct + 1) * P],
                                      band[:, 0:2 * P], start=True, stop=False)
                            last = pe.matmul(bank[2][:, col + P:col + SEQ], gate_sb[:, 1, ct * P:(ct + 1) * P],
                                             band[:, 2 * P:3 * P], start=False, stop=True)
                        last.then_inc(filled[2], 1)
                    if n == 10:
                        wait_read(pe, "q", 0, g)
                        for b in range(4):
                            wait_read(pe, "k", b)
                        scores(g, 1)
                        wait_read(pe, "window", 2, g)
                        claim("pool", 1, g)
                        for dt in range(2):
                            for ct in range(2):
                                last = pe.matmul(bank[1][:, dt * SEQ:(dt + 1) * SEQ], pool_w[:, ct, dt * P:(dt + 1) * P],
                                                 winT[:, ct, :], start=(ct == 0), stop=(ct == 1))
                        last.then_inc(filled[1], 1)
                    if n == 14:
                        prob_transposes(g, 1)
                    if n == 16:
                        for b in (2, 3):
                            wait_read(pe, "probT1", b, g)
                        prob_values(g, 1)
                        scores(g, 0)
                    if n == 17:
                        wait_strip_read(pe, "heads", g, 1)
                        strip_transposes("rk", 3, g, RKD)
                        strip_transposes("rq", 0, g, 0)
                    if n == 18:
                        wait_read(pe, "rk", 3, g)
                        wait_read(pe, "rq", 0, g)
                        claim("inner", 0, g)
                        for j, lo_q in ((0, 0), (1, P)):
                            for dt in range(2):
                                last = pe.matmul(bank[0][:, j * SEQ:j * SEQ + SEQ - lo_q], rkT[:, dt, j * P:(j + 1) * P],
                                                 rqT[:, dt, lo_q:SEQ], start=(dt == 0), stop=(dt == 1))
                        last.then_inc(filled[0], 1)
                    if n == 21:
                        prob_transposes(g, 0)
                    if n == 23:
                        wait_read(pe, "probT0", 2, g)
                        prob_values(g, 0)
                    if n == 25:
                        wait_strip_read(pe, "heads", g, 2)
                        wait_read(pe, "inner", 0, g)
                        claim("o", 2, g)
                        pe.matmul(bank[2][:, :], innerT[:, 0:P], gate_sb[:, 0, :], start=True, stop=True).then_inc(filled[2], 1)
                        claim("o", 3, g)
                        pe.matmul(bank[3][:, :], innerT[:, P:2 * P], gate_sb[:, 0, :], start=True, stop=False)
                        pe.matmul(bank[3][:, :], innerT[:, 2 * P:3 * P], gate_sb[:, 1, :], start=False, stop=True).then_inc(filled[3], 1)

            with pe.Fori(0, CH) as c:
                n = 0
                for br in range(3):
                    for k in range(GD):
                        products("merge", c, n, xT_hi, xT_lo, KG * k, 2 * br, k == 0, k == GD - 1)
                        if n == 3:
                            with pe.If(c < 1):
                                ret_transposes(KVH - 1)
                        n += 1
                    hi, lo = ((poolT_hi, poolT_lo), (attT_hi, attT_lo), (retT_hi, retT_lo))[br]
                    if br == 0:
                        wait_read(pe, "pool", 1, KVH - 1)
                    if br == 1:
                        wait_read(pe, "pv0", 1, KVH - 1)
                    if br == 2:
                        for b in range(2):
                            wait_read(pe, "ret", b, KVH - 1)
                    ng = GD if br == 2 else GH
                    for k in range(ng):
                        products("merge", c, n, hi, lo, KG * k, 2 * br + 1, k == 0, k == ng - 1)
                        n += 1
            wait_strip_read(pe, "merge", CH - 1, 5)
            transpose_chunks("merged", lambda c, m, k: merged[:, c, m, k * P:(k + 1) * P], lambda c: None)
            with pe.Fori(0, CH // 2) as i:
                for n in range(2 * GD):
                    k = n % GD
                    if n < GD:
                        wait_xT("merged", k)
                    products("out", i, n, xT_hi, xT_lo, KG * k, n // GD, k == 0, k == GD - 1)

            transpose_chunks("x2", h_chunk, lambda c: pe.wait_ge(h_ready, MT * (CH + c + 1)))
            swiglu(1)

        @block.scalar
        def _(act):
            def round_group(sec, i, n):
                ahead = n + SLOTS

                def round_it(block1=None):
                    s = n % SLOTS
                    act.wait_ge(w_landed[s], group_landed(sec, i, ahead))
                    if block1 is not None:
                        act.wait_ge(block1_landed[s], block1)
                    act.wait_ge(w_used, group(sec, i, ahead) + 1)
                    act.activation(w_hi[:, s, :], w_raw[:, s, :], ACT.Copy).then_inc(w_rounded, 1)

                if sec == "kv" and ahead >= GD:
                    round_it(block_landed(0, ahead - GD))
                elif sec == "heads" and ahead >= 4 * GD:
                    with act.If(i < KVH - 1):
                        round_it(block_landed(i + 1, ahead - 4 * GD))
                    with act.If(i > KVH - 2):
                        round_it()
                elif sec == "heads" and two_blocks(ahead):
                    round_it(block_landed(i, ahead))
                else:
                    round_it()

            def transposed_hi(name, gain):
                for k in range(0, KD, 2):
                    b, n = chunk_bank(k // 2)
                    wait_filled(act, name, b, n)
                    if gain is None:
                        last = act.activation(xT_hi[:, k:k + 2, :].rearrange("p k n -> p (k n)"), bank[b][:, :], ACT.Copy)
                    else:
                        for kk in range(2):
                            last = act.activation(xT_hi[:, k + kk, :], bank[b][:, kk * SEQ:(kk + 1) * SEQ], ACT.Copy,
                                                  scale=gain[:, k + kk:k + kk + 1])
                    last.then_inc(rounded[b], 1)

            def input_squares(blk):
                for m in range(MT):
                    act.wait_ge(squares, SQUARES[f"pre{blk}"] + m + 1)
                    act.activation(junk[:, :], h[:, m, :], ACT.Square, accum_out=sq_pre[:, m:m + 1]).then_inc(squares, 1)

            def hidden_hi(f, p):
                for m in range(MT):
                    wait_filled(act, f"hidden{f}", m, p)
                    act.activation(act_hi[:, ds(4 * p, 4), m * P:(m + 1) * P],
                                   bank[m][:, :].rearrange("p (k n) -> p k n", n=P), ACT.Copy).then_inc(rounded[m], 1)

            def output_squares(sec, i, n, k):
                wait_strip(act, sec, i, n)
                for m in range(MT):
                    act.wait_ge(squares, SQUARES[sec] + i * 2 * MT + k * MT + m + 1)
                    act.activation(junk[:, 0:STRIP], acc[pair_of(sec, k)][m][:, :], ACT.Square,
                                   accum_out=sq_strip[:, k, m:m + 1]).then_inc(squares, 1)

            def swiglu(f):
                sec = f"up{f}"
                with act.Fori(0, NUP) as i:
                    for n in range(2 * GD):
                        round_group(sec, i, n)
                        if n == 1:
                            with act.If(i > 0):
                                hidden_hi(f, before(i, NUP))
                        if n == 2:
                            with act.If(i < 1):
                                input_squares(2 * f)
                        if n == GD - 1:
                            wait_strip(act, sec, i, n)
                            if f == 0:
                                act.wait_ge(rs_ready, MEAN["pre0"] + 1)
                            else:
                                act.wait_ge(rs_ready, MEAN["pre2"] + 1)
                            pair = pair_of(sec, 0)
                            for m in range(MT):
                                last = act.activation(gate_sb[:, m, :], acc[pair][m][:, :], ACT.Silu,
                                                      scale=rs_pre[:, 2 * f, m:m + 1])
                            last.then_inc(acc_read[pair], 1)
                sec = f"down{f}"
                with act.Fori(0, CH // 2) as i:
                    for n in range(2 * GF):
                        if f == 1 and n >= 2 * GF - SLOTS:
                            with act.If(i < 1):
                                round_group(sec, i, n)
                        else:
                            round_group(sec, i, n)
                        if n == 1:
                            with act.If(i < 1):
                                hidden_hi(f, NUP - 1)
                        if n % GF == GF - 1:
                            output_squares(sec, i, n, n // GF)

            act.sem_inc(squares, 1)
            act.sem_inc(o_squares, 1)
            for n in range(SLOTS):
                round_group("up0", 0, n - SLOTS)
            act.wait_ge(consts_landed, 16 * NCONST)
            act.wait_ge(x_landed, 16)
            transposed_hi("x0", pre_gain[:, 0, :])
            swiglu(0)

            transposed_hi("x1", pre_gain[:, 1, :])
            for n in range(GD):
                round_group("kv", 0, n)
                if n == 2:
                    act.wait_ge(h_ready, MT * CH)
                    input_squares(1)
            for b in (0, 1):
                wait_filled(act, "k", b)
                act.activation(kT[:, 0, :, b * P:(b + 1) * P], bank[b][:, :].rearrange("p (g n) -> p g n", n=P),
                               ACT.Copy).then_inc(read[b], 1)

            def ret_hi(g):
                for half in range(2):
                    wait_filled(act, "ret", half, g)
                    for kk in range(2):
                        k = g * 4 + (2 * half + kk)
                        last = act.activation(retT_hi[:, ds(k, 1), :].rearrange("p a n -> p (a n)"),
                                              bank[half][:, kk * SEQ:(kk + 1) * SEQ], ACT.Copy, scale=ret_gain[:, ds(k, 1)])
                    last.then_inc(rounded[half], 1)

            def strip_out(g, n, k, func):
                wait_strip(act, "heads", g, n)
                act.wait_ge(rs_ready, MEAN["pre1"] + 1)
                pair = pair_of("heads", k)
                for m in range(MT):
                    last = act.activation(gate_sb[:, m, :], acc[pair][m][:, :], func, scale=rs_pre[:, 1, m:m + 1])
                last.then_inc(acc_read[pair], 1)

            def exps(g, m):
                act.wait_ge(max_ready, 2 * g + (1 if m == 1 else 2))
                w = P * (m + 1)
                for hd in range(QPK):
                    act.activation(s_sb[:, hd, 0:w], s_sb[:, hd, 0:w], ACT.Exp, bias=neg_max[:, hd:hd + 1],
                                   accum_out=den[:, hd:hd + 1])
                act.activation(sink_exp[:, :], sink_arg[:, :], ACT.Exp).then_inc(exp_done, 1)

            def att_hi(g, m):
                wait_filled(act, f"pv{m}", 1, g)
                act.activation(attT_hi[:, ds(2 * g, 2), m * P:(m + 1) * P],
                               bank[1][:, 0:2 * P].rearrange("p (k n) -> p k n", n=P), ACT.Copy).then_inc(rounded[1], 1)

            with act.Fori(0, KVH) as g:
                for n in range(4 * GD):
                    round_group("heads", g, n)
                    if n == 3:
                        with act.If(g > 0):
                            ret_hi(before(g, KVH))
                    if n == 7:
                        strip_out(g, n, 0, ACT.Copy)
                    if n == 8:
                        wait_filled(act, "q", 0, g)
                        act.activation(qT[:, :, :].rearrange("p k n -> p (k n)"), bank[0][:, :], ACT.Copy,
                                       scale=DH ** -0.5).then_inc(read[0], 1)
                    if n == 10:
                        wait_filled(act, "pool", 1, g)
                        for kk in range(2):
                            last = act.activation(poolT_hi[:, ds(2 * g + kk, 1), :].rearrange("p a n -> p (a n)"),
                                                  bank[1][:, kk * SEQ:(kk + 1) * SEQ], ACT.Copy,
                                                  scale=pool_gain[:, ds(2 * g + kk, 1)])
                        last.then_inc(rounded[1], 1)
                    if n == 11:
                        exps(g, 1)
                    if n == 14:
                        wait_filled(act, "probT1", 2, g)
                        act.activation(pT[:, 0:2, :].rearrange("p h n -> p (h n)"), bank[2][:, :], ACT.Copy).then_inc(read[2], 1)
                    if n == 16:
                        att_hi(g, 1)
                    if n == 17:
                        wait_filled(act, "rq", 0, g)
                        act.activation(rqT[:, :, :].rearrange("p k n -> p (k n)"), bank[0][:, :], ACT.Copy).then_inc(read[0], 1)
                    if n == 18:
                        exps(g, 0)
                    if n == 21:
                        wait_filled(act, "probT0", 2, g)
                        act.activation(pT[:, :, 0:P], bank[2][:, :].rearrange("p (h n) -> p h n", n=P), ACT.Copy).then_inc(read[2], 1)
                    if n == 23:
                        strip_out(g, n, 2, ACT.Copy)
                    if n == 24:
                        att_hi(g, 0)
                    if n == 26:
                        for m in range(MT):
                            wait_filled(act, "o", 2 + m, g)
                            act.wait_ge(o_squares, MT * g + m + 1)
                            act.activation(o_junk[:, :], bank[2 + m][:, :], ACT.Square,
                                           accum_out=sq_o[:, m:m + 1]).then_inc(o_squares, 1)
                    if n == 31:
                        strip_out(g, n, 3, ACT.Silu)

            with act.Fori(0, CH) as c:
                for n in range(4 * GD + 2 * GH):
                    round_group("merge", c, n)
                    if n == 3:
                        with act.If(c < 1):
                            ret_hi(KVH - 1)
                    if n in (7, 19, 31):
                        k = (7, 19, 31).index(n)
                        wait_strip(act, "merge", c, n)
                        if k:
                            wait_strip_read(act, "merge", c, 2 * k - 1)
                        pair = pair_of("merge", 2 * k)
                        for m in range(MT):
                            last = act.activation(gate_sb[:, m, :], acc[pair][m][:, :], ACT.Sigmoid,
                                                  scale=rs_pre[:, 1, m:m + 1])
                        last.then_inc(acc_read[pair], 1)
            transposed_hi("merged", None)
            with act.Fori(0, CH // 2) as i:
                for n in range(2 * GD):
                    round_group("out", i, n)
                    if n % GD == GD - 1:
                        output_squares("out", i, n, n // GD)

            transposed_hi("x2", pre_gain[:, 2, :])
            act.wait_ge(h_ready, 2 * MT * CH)
            swiglu(1)

        @block.vector
        def _(dve):
            step = {"base": 0, "n": 0}

            def link(ins, i=0, per=0):
                step["n"] += 1
                ins.then_inc(dve_step, 1)
                dve.wait_ge(dve_step, step["base"] + i * per + step["n"])

            def rest_group(sec, i, n):
                s = n % SLOTS
                dve.wait_ge(w_rounded, group(sec, i, n + SLOTS) + 1)
                dve.tensor_tensor(w_lo[:, s, :], w_raw[:, s, :], w_hi[:, s, :].bitcast(f32), ALU.subtract).then_inc(w_split, 1)

            def transposed_lo(name, c, gain):
                for k in (4 * c, 4 * c + 2):
                    b, n = chunk_bank(k // 2)
                    wait_rounded(dve, name, b, n)
                    if gain is None:
                        last = dve.tensor_tensor(xT_lo[:, k:k + 2, :].rearrange("p k n -> p (k n)"), bank[b][:, :],
                                                 xT_hi[:, k:k + 2, :].rearrange("p k n -> p (k n)").bitcast(f32), ALU.subtract)
                    else:
                        for kk in range(2):
                            last = dve.scalar_tensor_tensor(xT_lo[:, k + kk, :], bank[b][:, kk * SEQ:(kk + 1) * SEQ],
                                                            gain[:, k + kk:k + kk + 1], xT_hi[:, k + kk, :].bitcast(f32),
                                                            ALU.mult, ALU.subtract)
                    last.then_inc(read[b], 1)

            def hidden_lo(f, p):
                for m in range(MT):
                    wait_rounded(dve, f"hidden{f}", m, p)
                    hi = act_hi[:, ds(4 * p, 4), m * P:(m + 1) * P].bitcast(f32)
                    dve.tensor_tensor(act_lo[:, ds(4 * p, 4), m * P:(m + 1) * P],
                                      bank[m][:, :].rearrange("p (k n) -> p k n", n=P), hi, ALU.subtract).then_inc(read[m], 1)

            def strip_output(blk, sec, i, n, k):
                y = ys[blk]
                wait_strip(dve, sec, i, n)
                c = 2 * i + k
                for m in range(MT):
                    dve.wait_ge(squares, SQUARES[sec] + i * 2 * MT + k * MT + m + 2)
                    if m == MT - 1:
                        dve.wait_ge(sq_added, blk * CH + c + 1)
                        dve.tensor_tensor(sq_post[:, blk, :], sq_post[:, blk, :], sq_strip[:, k, :], ALU.add).then_inc(sq_added, 1)
                    last = dve.tensor_tensor(y[:, ds(c, 1), m, :].rearrange("p a n -> p (a n)"), acc[pair_of(sec, k)][m][:, :],
                                             post_gain[:, ds(c * STRIP, STRIP)], ALU.mult)
                last.then_inc(acc_read[pair_of(sec, k)], 1)

            def input_mean(blk):
                dve.wait_ge(squares, SQUARES[f"pre{blk}"] + MT + 1)
                dve.tensor_scalar(mean_sq[:, MEAN_ROW[f"pre{blk}"], :], sq_pre[:, :], 1.0 / D, EPS, ALU.mult, ALU.add).then_inc(mean_ready, 1)

            def residual(blk, half):
                dve.wait_ge(sq_added, CH * (blk + 1) + 1)
                scale = 4.0 if half else 1.0
                dve.tensor_scalar(mean_sq[:, MEAN_ROW[f"post{blk}"], :], sq_post[:, blk, :], scale / D, scale * EPS,
                                  ALU.mult, ALU.add).then_inc(mean_ready, 1)
                dve.wait_ge(rs_ready, MEAN[f"post{blk}"] + 1)
                for c in range(CH):
                    for m in range(MT):
                        hc = h[:, m, c * STRIP:(c + 1) * STRIP]
                        dve.scalar_tensor_tensor(hc, ys[blk][:, c, m, :], rs_post[:, blk, m:m + 1], hc,
                                                 ALU.mult, ALU.add).then_inc(h_ready, 1)
                    if blk < 2 and c >= 1:
                        transposed_lo(f"x{blk + 1}", c - 1, pre_gain[:, blk + 1, :])
                if blk < 2:
                    transposed_lo(f"x{blk + 1}", CH - 1, pre_gain[:, blk + 1, :])

            def swiglu(f):
                sec = f"up{f}"
                with dve.Fori(0, NUP) as i:
                    for n in range(2 * GD):
                        rest_group(sec, i, n)
                        if n == 1:
                            with dve.If(i > 0):
                                hidden_lo(f, before(i, NUP))
                        if n == 4:
                            with dve.If(i < 1):
                                input_mean(2 * f)
                    wait_strip(dve, sec, i, 2 * GD - 1)
                    wait_strip_read(dve, sec, i, 0)
                    for m in range(MT):
                        last = dve.scalar_tensor_tensor(hid_sb[:, m, :], acc[pair_of(sec, 1)][m][:, :], rs_pre[:, 2 * f, m:m + 1],
                                                        gate_sb[:, m, :], ALU.mult, ALU.mult)
                    last.then_inc(acc_read[pair_of(sec, 1)], 1)
                sec = f"down{f}"
                dve.wait_ge(gain_landed, 16 if f == 0 else 48)
                with dve.Fori(0, CH // 2) as i:
                    for n in range(2 * GF):
                        if f == 1 and n >= 2 * GF - SLOTS:
                            with dve.If(i < 1):
                                rest_group(sec, i, n)
                        else:
                            rest_group(sec, i, n)
                        if n == 1:
                            with dve.If(i < 1):
                                hidden_lo(f, NUP - 1)
                        if n % GF == GF - 1:
                            strip_output(2 * f, sec, i, n, n // GF)

            dve.sem_inc(w_split, SLOTS)
            dve.memset(sq_post[:, :, :], 0.0).then_inc(sq_added, 1)
            for n in range(SLOTS):
                rest_group("up0", 0, n - SLOTS)
            dve.wait_ge(consts_landed, 16 * NCONST)
            dve.tensor_scalar(neg_sink[:, :], sink[:, :], -1.0, None, ALU.mult).then_inc(setup_done, 1)
            for c in range(CH):
                transposed_lo("x0", c, pre_gain[:, 0, :])
            dve.wait_ge(setup_done, 2)
            swiglu(0)
            residual(0, True)

            for n in range(GD):
                rest_group("kv", 0, n)
                if n == 4:
                    input_mean(1)
            wait_strip(dve, "kv", 0, GD - 1)
            dve.wait_ge(rs_ready, MEAN["pre1"] + 1)
            dve.wait_ge(pads_zeroed, 2)
            for m in range(MT):
                kv = acc[pair_of("kv", 0)][m]
                dve.tensor_scalar(k_pad[:, m, :, DH:2 * DH], kv[:, 0:KVH * DH].rearrange("p (g n) -> p g n", n=DH),
                                  rs_pre[:, 1, m:m + 1], None, ALU.mult)
                last = dve.tensor_scalar(v_sb[:, m, :], kv[:, KVH * DH:STRIP], rs_pre[:, 1, m:m + 1], None, ALU.mult)
            last.then_inc(acc_read[pair_of("kv", 0)], 1)
            for b in (2, 3):
                wait_filled(dve, "k", b)
                dve.tensor_copy(kT[:, 1, :, (b - 2) * P:(b - 1) * P],
                                bank[b][:, :].rearrange("p (g n) -> p g n", n=P)).then_inc(read[b], 1)

            def ret_lo(g):
                for half in range(2):
                    wait_rounded(dve, "ret", half, g)
                    for kk in range(2):
                        k = g * 4 + (2 * half + kk)
                        last = dve.scalar_tensor_tensor(retT_lo[:, ds(k, 1), :].rearrange("p a n -> p (a n)"),
                                                        bank[half][:, kk * SEQ:(kk + 1) * SEQ], ret_gain[:, ds(k, 1)],
                                                        retT_hi[:, ds(k, 1), :].rearrange("p a n -> p (a n)").bitcast(f32),
                                                        ALU.mult, ALU.subtract)
                    last.then_inc(read[half], 1)

            LINKS = 9

            def biased_scores(g, m):
                w = P * (m + 1)
                per_bank = STRIP // w
                for hd in range(QPK):
                    b = 2 + hd // per_bank
                    if hd % per_bank == 0:
                        wait_filled(dve, f"score{m}", b, g)
                    last = dve.scalar_tensor_tensor(s_sb[:, hd, 0:w], dist[:, 2 * P - w:2 * P], neg_slope[:, ds(QPK * g + hd, 1)],
                                                    bank[b][:, (hd % per_bank) * w:(hd % per_bank + 1) * w], ALU.mult, ALU.add)
                    if (hd + 1) % per_bank == 0:
                        last.then_inc(read[b], 1)

            def maxima(g, m):
                w = P * (m + 1)
                last_bank = 3 if m == 1 else 2
                wait_read(dve, f"score{m}", last_bank, g)
                link(dve.tensor_reduce(neg_max[:, :], s_sb[:, :, 0:w], AX.X, ALU.max, negate=True), g, LINKS)
                link(dve.tensor_tensor(neg_max[:, :], neg_max[:, :], neg_sink[:, ds(QPK * g, QPK)], ALU.min), g, LINKS)
                dve.tensor_tensor(sink_arg[:, :], neg_max[:, :], sink[:, ds(QPK * g, QPK)], ALU.add).then_inc(max_ready, 1)

            def probabilities(g, m):
                w = P * (m + 1)
                dve.wait_ge(exp_done, 2 * g + (1 if m == 1 else 2))
                link(dve.tensor_tensor(den[:, :], den[:, :], sink_exp[:, :], ALU.add), g, LINKS)
                link(dve.reciprocal(rden[:, :], den[:, :]), g, LINKS)
                for hd in range(QPK):
                    last = dve.tensor_scalar(s_sb[:, hd, 0:w], s_sb[:, hd, 0:w], rden[:, hd:hd + 1], None, ALU.mult)
                last.then_inc(prob_ready, 1)

            def att_lo(g, m):
                wait_rounded(dve, f"pv{m}", 1, g)
                hi = attT_hi[:, ds(2 * g, 2), m * P:(m + 1) * P].bitcast(f32)
                dve.tensor_tensor(attT_lo[:, ds(2 * g, 2), m * P:(m + 1) * P],
                                  bank[1][:, 0:2 * P].rearrange("p (k n) -> p k n", n=P), hi, ALU.subtract).then_inc(read[1], 1)

            step["base"], step["n"] = step["base"] + step["n"], 0
            with dve.Fori(0, KVH) as g:
                link(dve.tensor_copy(v_now[:, :, DH:2 * DH], v_sb[:, :, ds(g * DH, DH)]), g, LINKS)
                for n in range(4 * GD):
                    rest_group("heads", g, n)
                    if n == 3:
                        with dve.If(g > 0):
                            ret_lo(before(g, KVH))
                    if n == 8:
                        wait_filled(dve, "window", 2, g)
                        dve.tensor_copy(winT[:, :, :].rearrange("p k n -> p (k n)"), bank[2][:, :]).then_inc(read[2], 1)
                    if n == 10:
                        biased_scores(g, 1)
                        maxima(g, 1)
                        wait_rounded(dve, "pool", 1, g)
                        for kk in range(2):
                            last = dve.scalar_tensor_tensor(poolT_lo[:, ds(2 * g + kk, 1), :].rearrange("p a n -> p (a n)"),
                                                            bank[1][:, kk * SEQ:(kk + 1) * SEQ], pool_gain[:, ds(2 * g + kk, 1)],
                                                            poolT_hi[:, ds(2 * g + kk, 1), :].rearrange("p a n -> p (a n)").bitcast(f32),
                                                            ALU.mult, ALU.subtract)
                        last.then_inc(read[1], 1)
                    if n == 12:
                        probabilities(g, 1)
                    if n == 14:
                        wait_filled(dve, "probT1", 3, g)
                        dve.tensor_copy(pT[:, 2:4, :].rearrange("p h n -> p (h n)"), bank[3][:, :]).then_inc(read[3], 1)
                    if n == 15:
                        wait_strip(dve, "heads", g, n)
                        pair = pair_of("heads", 1)
                        wait_filled(dve, "window", 2, g)
                        for m in range(MT):
                            last = dve.tensor_scalar(gate_sb[:, m, :], acc[pair][m][:, :], rs_pre[:, 1, m:m + 1], None, ALU.mult)
                        last.then_inc(acc_read[pair], 1)
                    if n == 16:
                        biased_scores(g, 0)
                        att_lo(g, 1)
                        maxima(g, 0)
                    if n == 17:
                        wait_filled(dve, "rk", 3, g)
                        dve.tensor_copy(rkT[:, :, :].rearrange("p k n -> p (k n)"), bank[3][:, :]).then_inc(read[3], 1)
                    if n == 18:
                        wait_filled(dve, "inner", 0, g)
                        dve.tensor_tensor(innerT[:, 0:SEQ], bank[0][:, 0:SEQ], decay[:, :], ALU.mult)
                        dve.tensor_tensor(innerT[:, SEQ:SEQ + P], bank[0][:, SEQ:SEQ + P], decay[:, 0:P], ALU.mult).then_inc(read[0], 1)
                    if n == 19:
                        probabilities(g, 0)
                    if n == 24:
                        att_lo(g, 0)
                    if n == 26:
                        for m in range(MT):
                            dve.wait_ge(o_squares, MT * g + m + 2)
                            dve.tensor_copy(hid_sb[:, m, :], bank[2 + m][:, :]).then_inc(read[2 + m], 1)
                        dve.tensor_scalar(mean_sq[:, MEAN_ROW["o"], :], sq_o[:, :], 1.0 / RVD, EPS, ALU.mult, ALU.add).then_inc(mean_ready, 1)
                wait_strip_read(dve, "heads", g, 3)
                dve.wait_ge(rs_ready, MEAN["o"] + g + 1)
                for m in range(MT):
                    last = dve.scalar_tensor_tensor(gate_sb[:, m, :], hid_sb[:, m, :], rs_o[:, m:m + 1], gate_sb[:, m, :],
                                                    ALU.mult, ALU.mult)
                last.then_inc(ret_ready, 1)
            per, step["base"] = step["n"], step["base"] + KVH * step["n"]
            assert per == LINKS, per
            step["n"] = 0

            MLINKS = 4
            with dve.Fori(0, CH) as c:
                for n in range(4 * GD + 2 * GH):
                    rest_group("merge", c, n)
                    if n == 3:
                        with dve.If(c < 1):
                            ret_lo(KVH - 1)
                    if n in (11, 23, 39):
                        k = (11, 23, 39).index(n)
                        wait_strip(dve, "merge", c, n)
                        wait_strip_read(dve, "merge", c, 2 * k)
                        pair = pair_of("merge", 2 * k + 1)
                        for m in range(MT):
                            mc = merged[:, ds(c, 1), m, :].rearrange("p a n -> p (a n)")
                            if k == 0:
                                last = dve.tensor_tensor(mc, acc[pair][m][:, :], gate_sb[:, m, :], ALU.mult)
                            else:
                                link(dve.tensor_tensor(hid_sb[:, m, :], acc[pair][m][:, :], gate_sb[:, m, :], ALU.mult), c, MLINKS)
                                last = dve.tensor_tensor(mc, mc, hid_sb[:, m, :], ALU.add)
                        last.then_inc(acc_read[pair], 1)
            assert step["n"] == MLINKS, step["n"]
            step["base"], step["n"] = step["base"] + CH * MLINKS, 0
            for c in range(CH):
                transposed_lo("merged", c, None)
            dve.wait_ge(gain_landed, 32)
            with dve.Fori(0, CH // 2) as i:
                for n in range(2 * GD):
                    rest_group("out", i, n)
                    if n % GD == GD - 1:
                        strip_output(1, "out", i, n, n // GD)
            residual(1, False)

            swiglu(1)
            residual(2, True)


_INS = ["x", "ffn1_pre", "ffn1_up", "ffn1_down", "ffn1_post", "mix_pre", "w_in", "pool_w", "pool_scale", "attn_sinks",
        "ret_norm", "w_pool_out", "w_attn_out", "w_ret_out", "w_gate", "w_out", "mix_post", "ffn2_pre", "ffn2_up",
        "ffn2_down", "ffn2_post"]


def _constants():
    import numpy as np
    p, q = np.arange(P)[:, None], np.arange(2 * P)[None, :]
    dist = p + P - q
    dist = np.where((dist >= 0) & (dist < P), dist, 1e30)
    slope = np.exp2(-8.0 * np.arange(1, HEADS + 1) / HEADS)
    log_g = np.log(1.0 - np.exp2(-5.0 - np.arange(KVH)))[:, None, None]
    decay = np.where(q >= p, np.exp(log_g * np.maximum(q - p, 0)), 0.0) * RKD ** -0.5
    s, t = np.arange(SEQ)[:, None], np.arange(SEQ)[None, :]
    band = []
    for w in POOL_WINDOWS:
        full = np.where((s <= t) & (s > t - w), 1.0 / np.minimum(t + 1, w), 0.0) - (s == t)
        band.append(np.concatenate([full[:P], full[P:, P:]], axis=1))
    consts = {"c_ident": np.eye(P), "c_dist": dist, "c_neg_slope": np.broadcast_to(-slope, (P, HEADS)),
              "c_decay": decay, "c_band": np.stack(band)}
    return {k: np.ascontiguousarray(v, dtype=np.float32) for k, v in consts.items()}


def kernel(**inputs):
    import numpy as _np
    import concourse.bacc as _bacc
    from concourse import mybir as _mybir
    from concourse.bass_utils import run_bass_kernel_spmd as _run

    nc = _bacc.Bacc("TRN2", target_bir_lowering=False, num_devices=1)
    arrays, args = {}, {}
    for name, a in [(n, inputs[n]) for n in _INS] + list(_constants().items()):
        a = _np.ascontiguousarray(a)
        arrays[f"in_{name}_dram"] = a
        args[name] = nc.dram_tensor(f"in_{name}_dram", a.shape, _mybir.dt.from_np(a.dtype), kind="ExternalInput").ap()
    out = nc.dram_tensor("out_0_dram", (1, SEQ, D), _mybir.dt.float32, kind="ExternalOutput").ap()
    hybrid_trunk(nc, args, out)
    r = _run(nc, [arrays], core_ids=[0])
    return r.results[0]["out_0_dram"]
```
